# Optimizing a Trainium2 kernel written in Bass

```python
import jax, jax.numpy as jnp
from jax import lax
import numpy as np

D_MODEL = 1024
BATCH = 1
SEQ = 1024
DEPTH = 1

CHUNK = 64
D_MIX = D_MODEL
D_CONV = D_MIX // 2
CONV_WIDTH = 3
N_HEADS = 8
HEAD_DIM = (D_MIX - D_CONV) // N_HEADS
D_ATTN = N_HEADS * HEAD_DIM
ROT_DIM = HEAD_DIM // 4
ROPE_THETA = 500000.0
IDX_HEADS = 4
IDX_DIM = 64
IDX_ROT_DIM = IDX_DIM // 4
INDEX_TOPK = 256
Q_BLOCK = 128
EPS = 1e-6

SPLIT_SIZES = (
    D_CONV, D_CONV, D_CONV, D_CONV,
    D_ATTN, D_ATTN, D_ATTN, D_ATTN,
    IDX_HEADS * IDX_DIM, IDX_DIM, IDX_HEADS,
)
PROJ_DIM = sum(SPLIT_SIZES)

kernel_name = "hybrid_shortconv_dsa_sandwich"

def rms_norm(x, g):
    xf = x.astype(jnp.float32)
    xf = xf * lax.rsqrt(jnp.mean(xf * xf, axis=-1, keepdims=True) + EPS)
    return (xf * g.astype(jnp.float32)).astype(x.dtype)

def rope_partial(x, pos, rot_dim):
    half = rot_dim // 2
    inv_freq = jnp.power(jnp.float32(ROPE_THETA), -jnp.arange(half, dtype=jnp.float32) / half)
    ang = pos.astype(jnp.float32)[:, None] * inv_freq[None, :]
    cos = jnp.cos(ang)[None, :, None, :]
    sin = jnp.sin(ang)[None, :, None, :]
    xr = x[..., :rot_dim].astype(jnp.float32)
    x1, x2 = xr[..., :half], xr[..., half:]
    rot = jnp.concatenate([x1 * cos - x2 * sin, x2 * cos + x1 * sin], axis=-1).astype(x.dtype)
    return jnp.concatenate([rot, x[..., rot_dim:]], axis=-1)

def short_conv_mixer(h, b_gate, c_gate, conv_w):
    u = c_gate * h
    rhs = conv_w.reshape(CONV_WIDTH, 1, D_CONV).astype(u.dtype)
    y = lax.conv_general_dilated(
        u, rhs, window_strides=(1,), padding=[(CONV_WIDTH - 1, 0)],
        dimension_numbers=("NWC", "WIO", "NWC"), feature_group_count=D_CONV)
    return b_gate * y

def sparse_indexed_attention(q, k, v, q_idx, k_idx, w_idx, pos, top_k):
    B, S, H, Dh = q.shape
    nblk = S // Q_BLOCK

    def to_blocks(a):
        return jnp.moveaxis(a.reshape((B, nblk, Q_BLOCK) + a.shape[2:]), 1, 0)

    def block_fn(args):
        qb, qib, wb, posb = args
        limit = (posb // CHUNK + 1) * CHUNK
        admissible = pos[None, :] < limit[:, None]
        logits = jnp.einsum("bqhd,bsd->bqhs", qib, k_idx,
                            preferred_element_type=jnp.float32) * (IDX_DIM ** -0.5)
        score = jnp.einsum("bqh,bqhs->bqs", wb.astype(jnp.float32) * (IDX_HEADS ** -0.5),
                           jax.nn.relu(logits))
        score = jnp.where(admissible[None], score, -jnp.inf)
        _, sel = lax.top_k(score, top_k)
        valid = sel < limit[None, :, None]
        kg = jax.vmap(lambda kk, ii: kk[ii])(k, sel)
        vg = jax.vmap(lambda vv, ii: vv[ii])(v, sel)
        att = jnp.einsum("bqhd,bqkhd->bqhk", qb, kg,
                         preferred_element_type=jnp.float32) * (HEAD_DIM ** -0.5)
        att = jnp.where(valid[:, :, None, :], att, -jnp.inf)
        p = jax.nn.softmax(att, axis=-1)
        return jnp.einsum("bqhk,bqkhd->bqhd", p.astype(vg.dtype), vg)

    out = lax.map(block_fn, (to_blocks(q), to_blocks(q_idx), to_blocks(w_idx),
                             pos.reshape(nblk, Q_BLOCK)))
    return jnp.moveaxis(out, 0, 1).reshape(B, S, H, Dh)

def setup_inputs(seed: int = 0) -> dict:
    key = jax.random.key(seed)
    ks = jax.random.split(key, 7)
    x = jax.random.normal(ks[0], (BATCH, SEQ, D_MODEL), jnp.float32)
    norm_pre_g = 1.0 + 0.05 * jax.random.normal(ks[1], (DEPTH, D_MODEL), jnp.float32)
    w_in = jax.random.normal(ks[2], (DEPTH, D_MODEL, PROJ_DIM), jnp.float32) * (D_MODEL ** -0.5)
    conv_w = jax.random.normal(ks[3], (DEPTH, CONV_WIDTH, D_CONV), jnp.float32) * (CONV_WIDTH ** -0.5)
    w_out = jax.random.normal(ks[4], (DEPTH, D_MIX, D_MODEL), jnp.float32) * (D_MIX ** -0.5)
    norm_post_g = 1.0 + 0.05 * jax.random.normal(ks[5], (DEPTH, D_MODEL), jnp.float32)
    return {"x": x, "norm_pre_g": norm_pre_g, "w_in": w_in, "conv_w": conv_w,
            "w_out": w_out, "norm_post_g": norm_post_g}

def reference(x, norm_pre_g, w_in, conv_w, w_out, norm_post_g):
    B, S, _ = x.shape
    top_k = min(INDEX_TOPK, S // 4)
    pos = jnp.arange(S, dtype=jnp.int32)
    split_idx = [int(i) for i in np.cumsum(SPLIT_SIZES)[:-1]]
    for l in range(DEPTH):
        xn = rms_norm(x, norm_pre_g[l])
        proj = jnp.einsum("bsd,dp->bsp", xn, w_in[l])
        (h, b_gate, c_gate, z_conv, q, k, v, z_attn,
         q_idx, k_idx, w_idx) = jnp.split(proj, split_idx, axis=-1)

        y_conv = short_conv_mixer(h, b_gate, c_gate, conv_w[l]) * jax.nn.silu(z_conv)

        q = rope_partial(q.reshape(B, S, N_HEADS, HEAD_DIM), pos, ROT_DIM)
        k = rope_partial(k.reshape(B, S, N_HEADS, HEAD_DIM), pos, ROT_DIM)
        v = v.reshape(B, S, N_HEADS, HEAD_DIM)
        q_idx = rope_partial(q_idx.reshape(B, S, IDX_HEADS, IDX_DIM), pos, IDX_ROT_DIM)
        k_idx = rope_partial(k_idx[:, :, None, :], pos, IDX_ROT_DIM)[:, :, 0, :]
        o = sparse_indexed_attention(q, k, v, q_idx, k_idx, w_idx, pos, top_k)
        y_attn = o.reshape(B, S, D_ATTN) * jax.nn.silu(z_attn)

        y = jnp.einsum("bsm,md->bsd", jnp.concatenate([y_conv, y_attn], axis=-1), w_out[l])
        x = x + rms_norm(y, norm_post_g[l])
    return x


_drawn_inputs = setup_inputs


def setup_inputs(seed=0):
    import zlib

    import numpy as np

    out = dict(_drawn_inputs(seed))
    spreads = {}
    factors = {}
    for name, (base, spread) in spreads.items():
        noise = np.random.default_rng([zlib.crc32(name.encode()), seed]).standard_normal(out[name].shape)
        drawn = base * np.exp(spread * noise) if base else spread * noise
        out[name] = __import__('jax').numpy.asarray(drawn.astype(out[name].dtype))
    for name, factor in factors.items():
        out[name] = (out[name] * factor).astype(out[name].dtype)
    return out
```

```python
from contextlib import ExitStack

import numpy as np

import concourse.bass as bass
from concourse import mybir

F32 = mybir.dt.float32
F32R = mybir.dt.float32r
BF16 = mybir.dt.bfloat16
I32 = mybir.dt.int32
I16 = mybir.dt.int16
U16 = mybir.dt.uint16
ALU = mybir.AluOpType
ACT = mybir.ActivationFunctionType

P = 128
SEQ, DM = 1024, 1024
TILES = SEQ // P
KB = DM // P
HALF = 512
CHUNK = 64
QKD, IQD = 6, 4
TOPK = 256
HD = 64
IH = 4
ROT = 16
RH = ROT // 2
DC = 512
CT = DC // P
PAIRS = DC // (2 * HD)
IDXC = IH * HD + HD + IH
FIRST_SEL = TOPK // P
BIG = 3.0e38
EPS = 1e-6
SCALE = HD ** -0.5
IDX_SCALE = (HD ** -0.5) * (IH ** -0.5)

CONV_COLS = (0, 2 * DC, 3 * DC, DC)
PAIR_COLS = (4 * DC, 5 * DC, 6 * DC, 7 * DC)
IDX_COL = 8 * DC

SEL_TILES = list(range(FIRST_SEL, TILES))
KEY_OFF = {}
_at = 0
for _i in SEL_TILES:
    KEY_OFF[_i] = _at
    _at += P * (_i + 1)
KEYS = _at
BIAS_OFF = [P * i * (i + 1) // 2 for i in range(TILES)]
BIAS_W = P * TILES * (TILES + 1) // 2
DVE_SEL = (7, 5)
ACT_SEL = (6, 4, 3, 2)
SEL_COL = {i: n for n, i in enumerate(DVE_SEL + ACT_SEL)}
NSEL = len(SEL_COL)
BITS = 16
DVE_KEYS = sum(P * (i + 1) for i in DVE_SEL)
ACT_KEYS = sum(P * (i + 1) for i in ACT_SEL)
JUNK_OFF = {}
for _sel in (DVE_SEL, ACT_SEL):
    _at = 0
    for _i in _sel:
        JUNK_OFF[_i] = _at
        _at += P * (_i + 1)
WO_RAW = 6
OUT = [(t, n) for t in range(TILES) for n in range(2)]
RELU = 6

UNITS = [(0, 0), (0, 1), (1, 0), (1, 1)]


FILL_FROM, FILL_TAIL = 4, 3
WO_FROM = 4
EARLY = 6
OUT_AHEAD = 6
FILL_WAIT = 5
INV_LAG = 0
T_RING = 3
AHEAD = 2
BLOCKS = [(u, j) for u, (_, g) in enumerate(UNITS) for j in range(4 * g + 4)]

DUP = [(a, w, hh) for a in range(2) for hh in range(2) for w in range(2)]


POOL_STEPS = "dddddwdwdpdpwppwpwwppppppppwpppw"
OPENING = "Z Z Z D0 D1 W D2 Z Z S0 Z Z Z S1 D3 Z S2 Z S3 D4 Z D5 D6 Z D7 Z Z S4 Z Z S5 G1"
LAST_OPENING = "Z Z W D0 Z D1 Z Z S0 D2 Z Z Z S1 D3 Z S2 Z S3 Z D4 D5 D6 Z D7 Z Z S4 Z Z S5 G1"


def opening_plan(opening=OPENING):
    z = [("Z", n, k) for n in range(2) for k in range(KB)]
    plan = []
    for step in opening.split():
        kind, n = step[0], int(step[1:] or 0)
        if kind == "Z":
            plan.append(z.pop(0))
            if plan[-1] == ("Z", 1, 2):
                plan.append(("G", 0, 0))
        else:
            plan.append((kind, n // 4, n) if kind == "S" else (kind, n, 0))
    assert not z
    return plan


def attention_plan():
    s_at = {0: [("S", 1, 6)], 1: [("S", 1, 7)]}
    for u in (2, 3):
        items = [("S", u, 4 * UNITS[u][1] + a) for a in range(4)]
        first = BLOCKS.index((u - 1, 0)) - (2 if u == 3 else 0)
        for a, item in enumerate(items):
            s_at.setdefault(first + a, []).append(item)
    core = [("T",) + BLOCKS[n] for n in range(AHEAD)]
    for n, (u, j) in enumerate(BLOCKS):
        if n + AHEAD < len(BLOCKS):
            core.append(("T",) + BLOCKS[n + AHEAD])
        core += s_at.get(n, [])
        core.append(("V", u, j))
        if j == 4 * UNITS[u][1] + 3:
            core.append(("O", u, 0))
    quanta = [("F", t, k) for t in range(TILES) for k in range(KB)]
    late = {n for u in (1, 3) for n in range(core.index(("S", u, 6)) - 1, core.index(("T", u, 0)))}
    weight = [0 if n < FILL_FROM or n >= len(core) - FILL_TAIL else FILL_WAIT if n in late else 1 for n in range(len(core))]
    plan, done, due = [], 0, []
    for n, item in enumerate(core):
        plan.append(item)
        while due and due[0][0] <= n:
            plan.append(due.pop(0)[1])
        want = -(-len(quanta) * sum(weight[:n + 1]) // sum(weight))
        while done < want:
            plan.append(quanta[done])
            _, t, k = quanta[done]
            if k == KB - 1:
                due.append((n + 1, ("C", t, 0)))
                if t % 4 == 3:
                    due.append((n + 3, ("R", t // 4, 0)))
            done += 1
    return plan + [d[1] for d in due]


PLAN = opening_plan() + attention_plan()
LAST_PLAN = opening_plan(LAST_OPENING) + attention_plan()
N_T = len(BLOCKS)
T_OF = {b: n for n, b in enumerate(BLOCKS)}
S_OF = {}
for _k, _u, _j in PLAN:
    if _k == "S":
        S_OF[(_u, _j)] = len(S_OF)
N_S = len(S_OF)
OUT_FROM = sum(1 for s in PLAN[:PLAN.index(("T", 3, 0))] if s[0] == "F") - EARLY
LAST_T = [T_OF[(u, 4 * g + 3)] + 1 for u, (_, g) in enumerate(UNITS)]


def build(nc, x, w_in, w_out, conv_w, g_pre, g_post, rope, out):
    ctx = ExitStack()
    base = [(nc.sbuf_base + 63) // 64 * 64]
    size = {F32: 4, F32R: 4, BF16: 2, I32: 4}

    def place(name, shape, dt, at=None):
        n = size[dt] * int(np.prod(shape[1:]))
        n = (n + 31) // 32 * 32
        off = base[0] if at is None else at
        if at is None:
            base[0] += n
        assert off + n <= nc.sbuf_usable_end, (name, off, n)
        t = nc.alloc_sbuf_tensor_at(name, shape, dt, offset=off)
        return t, off, off + n

    def sem(name):
        return ctx.enter_context(nc.semaphore(name))

    with ctx:
        xTh, o_xT, _ = place("xTh", [P, KB, SEQ], F32R)
        xTl, o_xTl, _ = place("xTl", [P, KB, SEQ], F32R)
        WH, o_WH, _ = place("WH", [P, 4, KB, P], F32R)
        WL, o_WL, _ = place("WL", [P, 4, KB, P], F32R)
        raw, _, _ = place("raw", [P, 2, HALF], F32)
        yb, o_yb, _ = place("yb", [P, PAIRS, SEQ], F32)
        qkv, o_qkv, e = place("qkv", [P, TILES, 3 * P], F32)
        gate, _, _ = place("gate", [P, 2, HALF], F32)
        bias, _, _ = place("bias", [P, BIAS_W], BF16)
        ident, _, _ = place("ident", [P, P], F32)
        cosT, _, _ = place("cosT", [P, TILES, RH], F32)
        sinT, _, _ = place("sinT", [P, TILES, RH], F32)
        wI, _, _ = place("wI", [P, TILES, IH], F32)
        cw, _, _ = place("cw", [P, CT, 3], F32)
        cwb, _, _ = place("cwb", [P, 3], F32)
        ss, _, _ = place("ss", [P, 2 * TILES], F32)
        std, _, _ = place("std", [P, TILES], F32)
        rstd, _, _ = place("rstd", [P, TILES], F32)
        epsT, _, _ = place("epsT", [P, 1], F32)
        zero, _, _ = place("zero", [P, 1], F32)
        cand, _, _ = place("cand", [P, NSEL], F32)
        cm, _, _ = place("cm", [P, NSEL], F32)
        step, _, _ = place("step", [P, NSEL], F32)
        cnt, _, _ = place("cnt", [P, NSEL], F32)
        thr, _, _ = place("thr", [P, NSEL], F32)
        ge, _, _ = place("ge", [P, NSEL], F32)
        nb, _, _ = place("nb", [P, NSEL], F32)
        need, _, _ = place("need", [P, NSEL], F32)
        sgs, _, _ = place("sgs", [P, NSEL], F32)
        nmax, _, _ = place("nmax", [P, TILES], F32)
        rsum, _, _ = place("rsum", [P, TILES], F32)
        rinv, _, _ = place("rinv", [P, TILES], F32)
        rtP, _, _ = place("rtP", [P, 2, 4 * 4 * RH], F32)
        R = base[0]

        xin, _, e = place("xin", [P, 2, DM], F32, R)
        xs, _, e = place("xs", [P, 2, DM], F32, e)
        iq, _, e = place("iq", [P, TILES, IDXC], F32, e)
        iqd, _, _ = place("iqd", [P, IQD, IH + 1, P], F32, e)
        WiR, _, e = place("WiR", [P, KB, IDXC], F32, e)
        WiH, _, e = place("WiH", [P, KB, IDXC], F32R, e)
        WiL, _, e = place("WiL", [P, KB, IDXC], F32R, e)
        QSI, _, e = place("QSI", [P, IH, SEQ], F32R, o_yb)
        KHI, _, e = place("KHI", [P, SEQ], F32R, o_qkv)
        KLI, _, e = place("KLI", [P, SEQ], F32R, e)
        sqj, _, e = place("sqj", [P, DM], F32, e)
        rtI, _, _ = place("rtI", [P, 2, 4 * 5 * RH], F32, e)
        gB, _, e = place("gB", [P, DM], F32, e)
        key, _, e = place("key", [P, KEYS], F32, R)
        R1 = R + 4 * BIAS_W
        hS, _, e = place("hS", [P, 2, HALF], F32, R1)
        uS, _, e = place("uS", [P, 2 + SEQ], F32, e)
        yS, _, e = place("yS", [P, 2, HALF], F32, e)
        tz, _, e = place("tz", [P, 2, HALF], F32, e)
        gz, _, e = place("gz", [P, 2, HALF], F32, e)
        yo, _, e = place("yo", [P, 2, HALF], F32, e)
        yh, _, e = place("yh", [P, 2, HALF], F32R, e)
        yl, _, e = place("yl", [P, 2, HALF], F32R, e)
        jd, _, e = place("jd", [P, DVE_KEYS], BF16, e)
        ja, _, e = place("ja", [P, ACT_KEYS], BF16, e)
        rl, _, e = place("rl", [P, RELU, HALF], F32, R1)
        kt, _, e = place("kt", [P, SEQ], I32, e)
        mS, _, e = place("mS", [P, 2, SEQ], F32, o_yb)
        mE, _, e = place("mE", [P, SEQ], F32, e)
        mC, _, e = place("mC", [P, SEQ], F32, e)
        kd, _, _ = place("kd", [P, 2, SEQ], F32, o_yb)
        PG1, _, e = place("PG1", [P, BIAS_W - BIAS_OFF[4]], F32, R)
        qkd, _, _ = place("qkd", [P, QKD, 4, P], F32, R)
        PG0, _, e = place("PG0", [P, BIAS_OFF[4]], F32, e)
        QS, _, e = place("QS", [P, 2, SEQ], F32R, e)
        KH, _, e = place("KH", [P, 2, SEQ], F32R, e)
        KL, _, e = place("KL", [P, 2, SEQ], F32R, e)
        VS, _, e = place("VS", [P, TILES, 4, HD], F32R, e)
        oL, _, e = place("oL", [P, HALF], F32, e)
        PTh, _, e = place("PTh", [P, T_RING, HALF], F32R, e)
        PTl, _, e = place("PTl", [P, T_RING, HALF], F32R, e)
        WOh, _, _ = place("WOh", [P, KB, DM], F32R, o_xT)
        WOl, _, _ = place("WOl", [P, KB, DM], F32R, o_xTl)
        wo_raw, _, _ = place("wo_raw", [P, WO_RAW, HALF], F32, o_qkv)
        ych, _, _ = place("ych", [P, CT, SEQ], F32R, o_WH)
        ycl, _, _ = place("ycl", [P, CT, SEQ], F32R, o_WL)
        xr, _, e = place("xr", [P, 2, DM], F32, R)
        oS, _, e = place("oS", [P, 2, DM], F32, e)
        gP, _, e = place("gP", [P, DM], F32, e)
        sqo, _, e = place("sqo", [P, 2, HALF], F32, e)
        yah, _, e = place("yah", [P, PAIRS, SEQ], F32R, e)
        yal, _, e = place("yal", [P, PAIRS, SEQ], F32R, e)
        spill_h = nc.dram_tensor("spill_h", (DC, SEQ), F32, kind="Internal").ap()
        spill_l = nc.dram_tensor("spill_l", (DC, SEQ), F32, kind="Internal").ap()

        banks = ctx.enter_context(nc.psum_tensor("banks", [P, 8, HALF], F32))
        pb = [banks[:, b, :] for b in range(8)]
        PPG = (PG0, PG1)

        names = """gains_loaded consts_loaded spilled
            ident_ready consts_ready squares std_ready rstd_ready xs_ready xT_psum xT_hi xT_lo
            idx_w_hi idx_w_lo idx_psum iq_ready wI_ready rope_step idup_psum idup_hi idup_lo
            logit_psum relu_ready first_score score_step key_step
            w_hi w_lo grp_psum h_ready bank_read conv_step y_ready y_hi y_lo
            sign_ready small_step kd_ready cand_ready counted sel_step
            qkv_psum qkv_ready z_psum v_hi v_lo tanh_ready gate_ready dup_psum dup_hi dup_lo
            s_psum s_masked p_ready p_sum_inv p_scaled t_psum t_hi t_lo pv_done
            ol_ready o_summed o_ready ya_hi ya_lo wo_hi wo_lo out_psum out_sq out_std out_rstd out_scaled out_ready
            taps_ready waited waited_dve dup_cols bias_ready diag_ready""".split()
        S = {n: sem(n) for n in names}
        xin_loaded = [sem(f"xin_loaded{b}") for b in range(2)]
        idx_w_loaded = [sem(f"idx_w_loaded{a}") for a in range(2)]
        raw_loaded = [sem(f"raw_loaded{b}") for b in range(2)]
        xr_loaded = [sem(f"xr_loaded{b}") for b in range(2)]
        conv_back_loaded = [sem(f"conv_back_loaded{b}") for b in range(2)]
        wo_loaded = [sem(f"wo_loaded{b}") for b in range(WO_RAW)]
        stored = [sem(f"stored{b}") for b in range(2)]

        block = ctx.enter_context(nc.Block())

        w_blk = w_in.rearrange("(k p) c -> p k c", p=P)
        wo_blk = w_out.rearrange("(k p) c -> p k c", p=P)
        raw4 = raw[:].rearrange("p b (k c) -> p b k c", k=4)
        n_w = 2 * 4

        def w_unit(it, m):
            return it * n_w + m

        GRP = 8
        CONV_HALVES = [(j, hf) for j in range(4) for hf in range(2)]
        PAIR_HALVES = [(j, hf) for hf in range(2) for j in range(3)] + [(3, 0), (3, 1)]

        IDUP = [(a, h) for a in range(2) for h in (IH, *range(IH))]
        LOGITS = [(i, h, c) for i in SEL_TILES for h in range(IH) for c in range((P * (i + 1) + HALF - 1) // HALF)]

        def steps_until(n, first):
            return sum(1 for _, h, _ in LOGITS[:n] if (h == 0) == first)

        def chunk(i, c):
            return c * HALF, min(P * (i + 1), (c + 1) * HALF)

        @block.sync
        def _(sp):
            sp.sem_inc(S["spilled"], 64)
            with nc.allow_non_contiguous_dma(reason="small tables"):
                for t in range(2):
                    sp.dma_start(xin[:, t, :], x[t * P:(t + 1) * P, :]).then_inc(xin_loaded[t], 16)
                    if t == 0:
                        sp.dma_start(gB[:], g_pre.to_broadcast((P, DM))).then_inc(S["gains_loaded"], 16)
                    sp.dma_start(WiR[:, 4 * t:4 * t + 4, :], w_blk[:, 4 * t:4 * t + 4, IDX_COL:IDX_COL + IDXC]).then_inc(idx_w_loaded[t], 16)
                sp.dma_start(cosT[:], rope[0].rearrange("(t p) f -> p t f", p=P)).then_inc(S["consts_loaded"], 16)
                sp.dma_start(sinT[:], rope[1].rearrange("(t p) f -> p t f", p=P)).then_inc(S["consts_loaded"], 16)
                for c in range(CT):
                    sp.dma_start(cw[:, c, :], conv_w[:, c * P:(c + 1) * P].rearrange("k p -> p k")).then_inc(S["consts_loaded"], 16)
            for t in range(2, TILES):
                sp.wait_ge(S["xs_ready"], t - 1)
                sp.dma_start(xin[:, t % 2, :], x[t * P:(t + 1) * P, :]).then_inc(xin_loaded[t % 2], 16)

            def load_w(it, cols, col0, halves=CONV_HALVES):
                for m, (j, hf) in enumerate(halves):
                    if not (isinstance(it, int) and it == 0 and m < 2):
                        sp.wait_ge(S["w_lo"], w_unit(it, m) - 1)
                    sp.dma_start(raw4[:, m % 2], w_blk[:, 4 * hf:4 * hf + 4, bass.ds(col0 + cols[j], P)]).then_inc(raw_loaded[m % 2], 16)

            def spill(it):
                for n in range(2):
                    sp.wait_ge(S["y_lo"], 2 * it + n + 1)
                    row = it * P
                    sp.dma_start(spill_h[bass.ds(row, P), n * HALF:(n + 1) * HALF], yh[:, n, :].bitcast(F32)).then_inc(S["spilled"], 16)
                    sp.dma_start(spill_l[bass.ds(row, P), n * HALF:(n + 1) * HALF], yl[:, n, :].bitcast(F32)).then_inc(S["spilled"], 16)

            load_w(0, CONV_COLS, 0)
            with sp.Fori(1, CT) as it:
                load_w(it, CONV_COLS, it * P)
                spill(it - 1)
            load_w(CT, PAIR_COLS, 0, PAIR_HALVES)
            spill(CT - 1)
            with sp.Fori(1, PAIRS) as p:
                load_w(p + CT, PAIR_COLS, p * P, PAIR_HALVES)
            for m in range(2 * KB):
                k, hf = divmod(m, 2)
                if m == 0:
                    sp.wait_ge(S["v_lo"], PAIRS)
                    sp.wait_ge(S["dup_cols"], TILES * (PAIRS + 1))
                elif m >= WO_RAW:
                    sp.wait_ge(S["wo_lo"], m - WO_RAW + 1)
                sp.dma_start(wo_raw[:, m % WO_RAW, :], wo_blk[:, k, hf * HALF:(hf + 1) * HALF]).then_inc(wo_loaded[m % WO_RAW], 16)
            sp.wait_ge(S["pv_done"], PAIRS * N_T)
            sp.wait_ge(S["o_ready"], 4 * PAIRS)
            with nc.allow_non_contiguous_dma(reason="gain on every partition"):
                sp.dma_start(gP[:], g_post.to_broadcast((P, DM))).then_inc(S["gains_loaded"], 16)
            def store(t):
                for n in range(2):
                    cols = slice(n * HALF, (n + 1) * HALF)
                    sp.wait_ge(S["out_ready"], 2 * t + n + 1)
                    sp.dma_start(out[t * P:(t + 1) * P, cols], oS[:, t % 2, cols]).then_inc(stored[t % 2], 16)

            for t in range(TILES):
                if t >= 2:
                    sp.wait_ge(S["out_ready"], 2 * (t - 1))
                sp.dma_start(xr[:, t % 2, :], x[t * P:(t + 1) * P, :]).then_inc(xr_loaded[t % 2], 16)
                if t >= 1:
                    store(t - 1)
            store(TILES - 1)
            for b in range(2):
                sp.wait_ge(stored[b], 32 * (TILES // 2))

        @block.gpsimd
        def _(pool):
            g = nc.gpsimd
            g.memset(ident[:], 0.0).then_inc(S["ident_ready"], 1)
            g.memset(epsT[:], EPS)
            g.memset(zero[:], 0.0).then_inc(S["consts_ready"], 1)
            pool.wait_ge(S["ident_ready"], 1)
            g.affine_select(out=ident[:], in_=ident[:], compare_op=ALU.not_equal, fill=1.0, base=0,
                            pattern=[[-1, P]], channel_multiplier=1).then_inc(S["ident_ready"], 1)
            for a in range(2):
                pool.wait_ge(idx_w_loaded[a], 16)
                g.tensor_scalar(WiH[:, 4 * a:4 * a + 4, :], WiR[:, 4 * a:4 * a + 4, :], 1.0, 1.0, ALU.mult, ALU.mult).then_inc(S["idx_w_hi"], 1)

            def split_w(it, m, half, free=None):
                j, hf = half
                pool.wait_ge(raw_loaded[m % 2], 16 * (it * (n_w // 2) + m // 2 + 1))
                if free is not None:
                    pool.wait_ge(S[free[0]], free[1])
                h = WH[:, j, 4 * hf:4 * hf + 4, :]
                pool.sem_inc(S["waited"], 1)
                g.tensor_scalar(h, raw4[:, m % 2], 1.0, 1.0, ALU.mult, ALU.mult).then_inc(S["w_hi"], 1)
                pool.wait_ge(S["w_hi"], w_unit(it, m) + 1)
                g.tensor_tensor(WL[:, j, 4 * hf:4 * hf + 4, :], raw4[:, m % 2], h.bitcast(F32), ALU.subtract).then_inc(S["w_lo"], 1)

            def double(dst, src, t, segs):
                g.tensor_scalar(dst.rearrange("p s (b d) -> p s b d", b=2),
                                src[:, t, 0:segs * HD].rearrange("p (s d) -> p s d", d=HD).unsqueeze(2).to_broadcast((P, segs, 2, HD)),
                                1.0, 1.0, ALU.mult, ALU.mult).then_inc(S["dup_cols"], 1)

            for m in range(2):
                split_w(0, m, CONV_HALVES[m])
            for t in range(TILES):
                pool.wait_ge(S["rope_step"], 6 * (t // 4 + 1))
                if t >= IQD:
                    pool.wait_ge(S["idup_psum"], IH + 1)
                double(iqd[:, t % IQD], iq, t, IH + 1)

            pool.wait_ge(S["wI_ready"], 1)
            split_w(0, 2, CONV_HALVES[2])
            split_w(0, 3, CONV_HALVES[3])
            for m, i in enumerate(SEL_TILES, 4):
                if m < n_w:
                    split_w(0, m, CONV_HALVES[m])
                for n, (ii, h, c) in enumerate(LOGITS):
                    if ii == i and h == 0:
                        c0, c1 = chunk(i, c)
                        pool.wait_ge(S["relu_ready"], n + 1)
                        g.tensor_scalar(key[:, KEY_OFF[i] + c0:KEY_OFF[i] + c1], rl[:, n % RELU, 0:c1 - c0], wI[:, i, 0:1], 1.0,
                                        ALU.mult, ALU.mult).then_inc(S["first_score"], 1)
            with pool.Fori(1, CT) as it:
                for m, (j, hf) in enumerate(CONV_HALVES):
                    split_w(it, m, (j, hf), ("grp_psum", (it - 1) * GRP + 2 * j + 2) if hf == 0 else None)
            for m, (j, hf) in enumerate(PAIR_HALVES):
                split_w(CT, m, (j, hf), ("grp_psum", (CT - 1) * GRP + 2 * j + 2))

            def scale(p, n, u, i):
                L = P * (i + 1)
                gg = UNITS[u][1]
                at = BIAS_OFF[i] - BIAS_OFF[4 * gg]
                pool.wait_ge(S["p_sum_inv"], p * N_S + n + 1)
                pool.sem_inc(S["waited"], 1)
                g.tensor_scalar(PPG[gg][:, at:at + L], PPG[gg][:, at:at + L], rinv[:, i:i + 1], 1.0,
                                ALU.mult, ALU.mult).then_inc(S["p_scaled"], 1)

            def double_pair(p, tiles):
                for t in tiles:
                    pool.wait_ge(S["rope_step"], 12 + 12 * p + 6 * (t // 4 + 1))
                    if t == 0:
                        pool.wait_ge(S["t_psum"], p * N_T)
                    if t >= QKD:
                        pool.wait_ge(S["dup_psum"], 8 * p + 4)
                    pool.sem_inc(S["waited"], 1)
                    double(qkd[:, t % QKD], qkv, t, 4)

            scales = list(S_OF.items())

            def scale_some(p, n0, n1):
                for (u, i), n in scales[n0:n1]:
                    scale(p, n, u, i)

            pool.wait_ge(S["bias_ready"], NSEL)
            with pool.Fori(0, PAIRS - 1) as p:
                def split_next(m):
                    free = {0: ("qkv_psum", TILES * (p + 1)), 6: ("z_psum", 2 * p + 2)}.get(m)
                    split_w(p + CT + 1, m, PAIR_HALVES[m], free)

                doubled = scaled = split = 0
                for step in POOL_STEPS:
                    if step == "d":
                        double_pair(p, [doubled])
                        doubled += 1
                    if step == "w":
                        split_next(split)
                        split += 1
                    if step == "p":
                        scale_some(p, scaled, scaled + 1)
                        scaled += 1
            double_pair(PAIRS - 1, range(TILES))
            lo_after = {7: 2, 8: 2, 11: EARLY - 4, 15: 2 * KB - EARLY}
            m = 0
            for (u, i), n in scales:
                scale(PAIRS - 1, n, u, i)
                for _ in range(lo_after.get(n, 0)):
                    k, hf = divmod(m, 2)
                    cols = slice(hf * HALF, (hf + 1) * HALF)
                    pool.wait_ge(S["wo_hi"], m + 1)
                    g.tensor_tensor(WOl[:, k, cols], wo_raw[:, m % WO_RAW, :], WOh[:, k, cols].bitcast(F32),
                                    ALU.subtract).then_inc(S["wo_lo"], 1)
                    m += 1

        def conv_bank(gi):
            return pb[(gi + 4) % 8]

        def t_bank(n):
            return pb[5 + n % T_RING]

        O_BANK = 4

        def s_bank(i):
            return 2 + (i % 2 if i < 4 else 0)

        def out_bank(g_i):
            return pb[(0, 1, 2, 3, 5, 6, 7, O_BANK)[g_i % 8]]

        @block.tensor
        def _(pe):
            mm = nc.tensor.matmul

            def three(acc, hi, lo, lhs_hi, lhs_lo, k, nk):
                mm(acc, lhs_hi, hi, start=(k == 0), stop=False)
                mm(acc, lhs_hi, lo, start=False, stop=False)
                return mm(acc, lhs_lo, hi, start=False, stop=(k == nk - 1))

            def idx_proj(t):
                pe.wait_ge(S["xT_lo"], 2 * t + 2)
                if t >= 2:
                    pe.wait_ge(S["iq_ready"], t - 1)
                rows = slice(t * P, (t + 1) * P)
                for k in range(KB):
                    if t == 0 and k % 4 == 0:
                        pe.wait_ge(S["idx_w_lo"], k // 4 + 1)
                    last = three(pb[4 + t % 2][:, 0:IDXC], WiH[:, k, :], WiL[:, k, :], xTh[:, k, rows], xTl[:, k, rows], k, KB)
                last.then_inc(S["idx_psum"], 1)

            pe.wait_ge(S["ident_ready"], 2)
            for t in range(TILES):
                pe.wait_ge(S["xs_ready"], t + 1)
                for b in range(2):
                    n = 2 * t + b
                    if n >= 4:
                        pe.wait_ge(S["xT_lo"], n - 3)
                    for k in range(4):
                        last = nc.tensor.transpose(pb[n % 4][:, k * P:(k + 1) * P], xs[:, t % 2, (4 * b + k) * P:(4 * b + k + 1) * P], ident[:])
                    last.then_inc(S["xT_psum"], 1)
                if t >= 1:
                    idx_proj(t - 1)
            idx_proj(TILES - 1)
            def idx_dup(n):
                a, h = IDUP[n]
                pe.wait_ge(S["dup_cols"], 4 * (a + 1))
                if n >= 2:
                    pe.wait_ge(S["idup_lo"], n - 1)
                for tt in range(4):
                    last = nc.tensor.transpose(pb[6 + n % 2][:, tt * P:(tt + 1) * P], iqd[:, (4 * a + tt) % IQD, h, :], ident[:])
                last.then_inc(S["idup_psum"], 1)

            def logits(n):
                i, h, c = LOGITS[n]
                c0, c1 = chunk(i, c)
                if n == 0:
                    pe.wait_ge(S["idup_lo"], len(IDUP))
                if n >= 4:
                    pe.wait_ge(S["relu_ready"], n - 3)
                acc = pb[n % 4][:, 0:c1 - c0]
                mm(acc, QSI[:, h, i * P:(i + 1) * P], KHI[:, c0:c1], start=True, stop=False)
                mm(acc, QSI[:, h, i * P:(i + 1) * P], KLI[:, c0:c1], start=False, stop=True).then_inc(S["logit_psum"], 1)

            def conv_group(it, gi, between=None):
                j, n = divmod(gi, 2)
                if n == 0:
                    pe.wait_ge(S["w_lo"], w_unit(it, 2 * j + 2))
                cols = slice(n * HALF, (n + 1) * HALF)
                for k in range(KB):
                    last = three(conv_bank(gi), xTh[:, k, cols], xTl[:, k, cols], WH[:, j, k, :], WL[:, j, k, :], k, KB)
                    if k == KB - 1:
                        last.then_inc(S["grp_psum"], 1)
                    if between:
                        between(k)

            def conv_body(it):
                for gi in range(GRP):
                    j, n = divmod(gi, 2)
                    if j == 0:
                        pe.wait_ge(S["h_ready"], (it - 1) * 2 + n + 1)
                    else:
                        pe.wait_ge(S["bank_read"], (it - 1) * 6 + gi - 1)
                    conv_group(it, gi)

            pe.wait_ge(S["iq_ready"], TILES)
            idup_at = {0: [0], 1: [1], 2: [2], 3: [3], 4: [4], 9: [5], 10: [6], 11: [7], 12: [8], 13: [9]}
            for gi in range(2):
                def transposes(k, gi=gi):
                    for n in idup_at.get(8 * gi + k, ()):
                        idx_dup(n)
                conv_group(0, gi, transposes)
            pe.wait_ge(S["idup_lo"], len(IDUP))
            per = -(-len(LOGITS) // (2 * KB))
            for gi in range(2, 4):
                def scores(k, gi=gi):
                    at = ((gi - 2) * KB + k) * per
                    for n in range(at, min(at + per, len(LOGITS))):
                        logits(n)
                conv_group(0, gi, scores)
            pe.wait_ge(S["relu_ready"], len(LOGITS))
            for gi in range(4, GRP):
                conv_group(0, gi)
            with pe.Fori(1, CT) as it:
                conv_body(it)

            def project(p, t, k, first=False):
                if k == 0:
                    if t >= 2:
                        pe.wait_ge(S["qkv_ready"], p * TILES + t - 1)
                    elif first:
                        pe.wait_ge(S["bank_read"], 6 * CT - 2)
                    else:
                        pe.wait_ge(S["gate_ready"], 2 * p + t - 1)
                if t == 0 and k % 4 == 0:
                    pe.wait_ge(S["w_lo"], w_unit(p + CT, 3 * (k // 4) + 3))
                rows = slice(t * P, (t + 1) * P)
                acc = pb[t % 2][:, 0:3 * P].rearrange("p (s c) -> p s c", s=3)
                last = three(acc, WH[:, 0:3, k, :], WL[:, 0:3, k, :], xTh[:, k, rows], xTl[:, k, rows], k, KB)
                if k == KB - 1:
                    last.then_inc(S["qkv_psum"], 1)

            def project_gate(p, n, k):
                if k == 0:
                    pe.wait_ge(S["qkv_ready"], p * TILES + TILES - 1 + n)
                if n == 0 and k == 0:
                    pe.wait_ge(S["w_lo"], w_unit(p + CT, 8))
                cols = slice(n * HALF, (n + 1) * HALF)
                last = three(pb[n][:], xTh[:, k, cols], xTl[:, k, cols], WH[:, 3, k, :], WL[:, 3, k, :], k, KB)
                if k == KB - 1:
                    last.then_inc(S["z_psum"], 1)

            def pair_body(p, fill):
                scored = False
                for kind, u, j in PLAN if fill else LAST_PLAN:
                    if kind == "Z":
                        project_gate(p, u, j)
                    if kind == "F" and fill:
                        project(p + 1, u, j)
                    if kind == "F" and not fill and len(out_done) < len(out_quanta):
                        g_i, kk = out_quanta[len(out_done)]
                        if u * KB + j >= OUT_FROM and len(out_done) < EARLY or scored:
                            if kk == 0 and g_i == 0:
                                pe.wait_ge(S["gate_ready"], 2 * PAIRS)
                            if not out_done[EARLY:] and scored:
                                pe.wait_ge(S["s_masked"], PAIRS * N_S)
                            out_step(g_i, kk, False)
                            out_done.append((g_i, kk))
                    scored = scored or (kind, u, j) == ("T", 3, 0)
                    if kind == "D":
                        a, w, hh = DUP[u]
                        pe.wait_ge(S["dup_cols"], TILES + p * TILES + 4 * (a + 1))
                        if u >= T_RING:
                            pe.wait_ge(S["dup_lo"], p * len(DUP) + u - T_RING + 1)
                        for tt in range(4):
                            last = nc.tensor.transpose(t_bank(u)[:, tt * P:(tt + 1) * P],
                                                       qkd[:, (4 * a + tt) % QKD, 2 * w + hh, :], ident[:])
                        last.then_inc(S["dup_psum"], 1)
                    if kind == "S":
                        hh, gg = UNITS[u]
                        n = S_OF[(u, j)]
                        if n == 0:
                            pe.wait_ge(S["dup_lo"], p * len(DUP) + 2)
                        if u == 1 and j == 4:
                            pe.wait_ge(S["dup_lo"], (p + 1) * len(DUP))
                        if n >= 1:
                            pe.wait_ge(S["s_masked"], p * N_S + (n - 1 if gg == 0 and j >= 2 else n))
                        L = P * (j + 1)
                        for c in range((L + HALF - 1) // HALF):
                            c0, c1 = c * HALF, min(L, (c + 1) * HALF)
                            acc = pb[s_bank(j) + c][:, 0:c1 - c0]
                            mm(acc, QS[:, hh, j * P:(j + 1) * P], KH[:, hh, c0:c1], start=True, stop=False)
                            last = mm(acc, QS[:, hh, j * P:(j + 1) * P], KL[:, hh, c0:c1], start=False, stop=True)
                        last.then_inc(S["s_psum"], 1)
                    if kind == "T":
                        gg = UNITS[u][1]
                        n = T_OF[(u, j)]
                        if j == 0:
                            pe.wait_ge(S["p_scaled"], p * N_S + 4 * (u + 1))
                        if n >= T_RING:
                            pe.wait_ge(S["t_lo"], p * N_T + n - T_RING + 1)
                        else:
                            pe.wait_ge(S["dup_lo"], (p + 1) * len(DUP))
                        for i in range(max(j, 4 * gg), 4 * gg + 4):
                            at = BIAS_OFF[i] - BIAS_OFF[4 * gg] + j * P
                            last = nc.tensor.transpose(t_bank(n)[:, (i - 4 * gg) * P:(i - 4 * gg + 1) * P],
                                                       PPG[gg][:, at:at + P], ident[:])
                        last.then_inc(S["t_psum"], 1)
                    if kind == "V":
                        hh, gg = UNITS[u]
                        n = T_OF[(u, j)]
                        c0 = max(j - 4 * gg, 0) * P
                        if n == 0:
                            pe.wait_ge(S["v_lo"], p + 1)
                        elif j == 0:
                            pe.wait_ge(S["o_summed"], p * 4 + u)
                        pe.wait_ge(S["t_lo"], p * N_T + n + 1)
                        acc = pb[O_BANK][:, c0:HALF]
                        nj = 4 * gg + 4
                        v = VS[:, j, 2 * hh:2 * hh + 2, :].rearrange("p a d -> p (a d)")
                        mm(acc, v, PTh[:, n % T_RING, c0:HALF], start=(j == 0), stop=False)
                        mm(acc, v, PTl[:, n % T_RING, c0:HALF], start=False, stop=(j == nj - 1)).then_inc(S["pv_done"], 1)

            def out_step(g_i, kk, attn):
                t, n = OUT[g_i]
                cols = slice(n * HALF, (n + 1) * HALF)
                rows = slice(t * P, (t + 1) * P)
                yhT, ylT = (yah, yal) if attn else (ych, ycl)
                k = kk + CT * attn
                if t == 0:
                    pe.wait_ge(S["wo_lo"], 2 * k + n + 1)
                if g_i == 0 and not attn:
                    pe.wait_ge(conv_back_loaded[kk // 3], 32)
                last = three(out_bank(g_i), WOh[:, k, cols], WOl[:, k, cols], yhT[:, kk, rows], ylT[:, kk, rows], k, KB)
                if k == KB - 1:
                    last.then_inc(S["out_psum"], 1)

            def out_half(g_i, attn):
                if attn and g_i % 4 == 0:
                    pe.wait_ge(S["ya_lo"], g_i // 4 + 1)
                if not attn and g_i == 4:
                    pe.wait_ge(S["t_lo"], PAIRS * N_T)
                if not attn and g_i >= 8:
                    pe.wait_ge(S["out_scaled"], g_i - 7)
                for kk in range(CT):
                    out_step(g_i, kk, attn)

            out_quanta = [(g2 + n, kk) for g2 in (0, 2) for kk in range(CT) for n in range(2)]
            out_done = []

            for t in range(TILES):
                for k in range(KB):
                    project(0, t, k, True)
            with pe.Fori(0, PAIRS - 1) as p:
                pair_body(p, True)
            pair_body(PAIRS - 1, False)
            for g_i, kk in out_quanta[len(out_done):]:
                out_step(g_i, kk, False)
            for g_i in range(4, OUT_AHEAD):
                out_half(g_i, False)
            for g_i in range(len(OUT)):
                if g_i >= OUT_AHEAD:
                    out_half(g_i, False)
                out_half(g_i, True)

        @block.scalar
        def _(act):
            A = nc.scalar.activation

            def square(t):
                act.wait_ge(xin_loaded[t % 2], 16 * (t // 2 + 1))
                if t >= 1:
                    act.wait_ge(S["squares"], t)
                A(sqj[:], xin[:, t % 2, :], ACT.Square, accum_out=ss[:, t:t + 1]).then_inc(S["squares"], 1)
                act.wait_ge(S["squares"], t + 1)
                A(std[:, t:t + 1], ss[:, t:t + 1], ACT.Sqrt, bias=epsT[:], scale=1.0 / DM).then_inc(S["std_ready"], 1)

            def copy_idx(t):
                act.wait_ge(S["idx_psum"], t + 1)
                A(iq[:, t, :], pb[4 + t % 2][:, 0:IDXC], ACT.Copy).then_inc(S["iq_ready"], 1)

            nc.scalar.preload_act_table(ACT.Sqrt)
            act.wait_ge(S["consts_ready"], 1)
            square(0)
            for t in range(TILES):
                if t + 1 < TILES:
                    square(t + 1)
                for b in range(2):
                    n = 2 * t + b
                    act.wait_ge(S["xT_psum"], n + 1)
                    A(xTh[:, 4 * b:4 * b + 4, t * P:(t + 1) * P], pb[n % 4][:].rearrange("p (k s) -> p k s", k=4), ACT.Copy).then_inc(S["xT_hi"], 1)
                if t >= 1:
                    copy_idx(t - 1)
            copy_idx(TILES - 1)
            for n, (a, h) in enumerate(IDUP):
                act.wait_ge(S["idup_psum"], n + 1)
                dst = KHI[:, a * HALF:(a + 1) * HALF] if h == IH else QSI[:, h, a * HALF:(a + 1) * HALF]
                A(dst, pb[6 + n % 2][:], ACT.Copy).then_inc(S["idup_hi"], 1)
            for n, (i, h, c) in enumerate(LOGITS):
                c0, c1 = chunk(i, c)
                act.wait_ge(S["logit_psum"], n + 1)
                if n >= RELU:
                    first = LOGITS[n - RELU][1] == 0
                    act.wait_ge(S["first_score"] if first else S["score_step"], steps_until(n - RELU + 1, first))
                A(rl[:, n % RELU, 0:c1 - c0], pb[n % 4][:, 0:c1 - c0], ACT.Relu, scale=IDX_SCALE).then_inc(S["relu_ready"], 1)

            def count(step_no, low):
                act.wait_ge(S["cand_ready"], step_no + (2 if low else 1))
                for i in ACT_SEL:
                    L, at, c, jo = P * (i + 1), KEY_OFF[i], SEL_COL[i], JUNK_OFF[i]
                    src = key[:, at:at + L] if low else key[:, at:at + L].bitcast(I16)[:, 1::2]
                    last = A(ja[:, jo:jo + L], src, ACT.Sign, bias=nb[:, c:c + 1], accum_out=cnt[:, c:c + 1])
                last.then_inc(S["counted"], 1)

            def conv_body(it, low):
                for gi in range(GRP):
                    j, n = divmod(gi, 2)
                    count(it * GRP + gi, low)
                    if j in (0, 2):
                        act.wait_ge(S["grp_psum"], it * GRP + gi + 1)
                        if j == 0:
                            A(hS[:, n, :], conv_bank(gi), ACT.Copy).then_inc(S["h_ready"], 1)
                        else:
                            A(tz[:, n, :], conv_bank(gi), ACT.Tanh, scale=0.5).then_inc(S["tanh_ready"], 1)
                    if j == 3:
                        act.wait_ge(S["y_ready"], 2 * it + n + 1)
                        act.wait_ge(S["spilled"], (it + 1) * 64)
                        A(yh[:, n, :], yo[:, n, :], ACT.Copy).then_inc(S["y_hi"], 1)

            act.wait_ge(S["key_step"], 3 * NSEL)
            nc.scalar.preload_act_table(ACT.Exp)
            with act.Fori(0, CT // 2) as it:
                conv_body(it, False)
            act.wait_ge(S["small_step"], 3 + 5 * BITS)
            for n, i in enumerate(SEL_TILES):
                L, k0, c = P * (i + 1), KEY_OFF[i], SEL_COL[i]
                if n >= 2:
                    act.wait_ge(S["key_step"], 3 * NSEL + n - 1)
                A(kd[:, n % 2, 0:L], key[:, k0:k0 + L].bitcast(I16)[:, 1::2], ACT.Identity, bias=need[:, c:c + 1],
                  scale=65536.0).then_inc(S["kd_ready"], 1)
            nc.scalar.preload_act_table(ACT.Exp)
            with act.Fori(CT // 2, CT) as it:
                conv_body(it, True)

            def sign_keys(n):
                i = SEL_TILES[n]
                L, k0, c = P * (i + 1), KEY_OFF[i], SEL_COL[i]
                if n == 0:
                    act.wait_ge(S["cand_ready"], 2 * BITS + 2)
                if n >= 2:
                    act.wait_ge(S["bias_ready"], n - 1)
                A(mS[:, n % 2, 0:L], key[:, k0:k0 + L], ACT.Sign, bias=nb[:, c:c + 1], accum_out=sgs[:, c:c + 1]).then_inc(S["sign_ready"], 1)

            def copy_qkv(p, t):
                act.wait_ge(S["qkv_psum"], p * TILES + t + 1)
                A(qkv[:, t, :], pb[t % 2][:, 0:3 * P], ACT.Copy).then_inc(S["qkv_ready"], 1)

            def exponent(p, n, u, j):
                gg = UNITS[u][1]
                at, L = BIAS_OFF[j] - BIAS_OFF[4 * gg], P * (j + 1)
                act.wait_ge(S["s_masked"], p * N_S + n + 1)
                A(PPG[gg][:, at:at + L], PPG[gg][:, at:at + L], ACT.Exp, bias=nmax[:, j:j + 1], scale=-1.0,
                  accum_out=rsum[:, j:j + 1]).then_inc(S["p_ready"], 1)

            def pair_body(p, fill):
                pend = None
                for kind, u, j in PLAN if fill else LAST_PLAN:
                    if kind in "ZFV" or (kind in "CR" and not fill) or kind == "R":
                        continue
                    exp_now, pend = pend, None
                    if exp_now and (kind == "S" or kind == "T" and j == 0):
                        exponent(p, *exp_now)
                        exp_now = None
                    if kind == "C" and fill:
                        if u == 0:
                            act.wait_ge(S["v_lo"], p + 1)
                            act.wait_ge(S["dup_cols"], TILES * (p + 2))
                        copy_qkv(p + 1, u)
                    if kind == "W":
                        act.wait_ge(S["qkv_ready"], TILES * (p + 1))
                        A(VS[:, :, 0::3, :], qkv[:, :, 2 * P:3 * P].rearrange("p t (h d) -> p t h d", h=2), ACT.Copy).then_inc(S["v_hi"], 1)
                    if kind == "G":
                        act.wait_ge(S["z_psum"], 2 * p + u + 1)
                        act.wait_ge(S["o_ready"], 4 * p)
                        A(gate[:, u, :], pb[u][:], ACT.Tanh, scale=0.5).then_inc(S["tanh_ready"], 1)
                        if not fill and u == 1:
                            conv_back(1, slice(3, 4))
                    if kind == "D":
                        a, w, hh = DUP[u]
                        act.wait_ge(S["dup_psum"], p * len(DUP) + u + 1)
                        A((QS, KH)[w][:, hh, a * HALF:(a + 1) * HALF], t_bank(u)[:], ACT.Copy).then_inc(S["dup_hi"], 1)
                    if kind == "S":
                        pend = (S_OF[(u, j)], u, j)
                    if kind == "T":
                        gg = UNITS[u][1]
                        n = T_OF[(u, j)]
                        c0 = max(j - 4 * gg, 0) * P
                        act.wait_ge(S["t_psum"], p * N_T + n + 1)
                        if n >= T_RING:
                            act.wait_ge(S["pv_done"], p * N_T + n - T_RING + 1)
                        A(PTh[:, n % T_RING, c0:HALF], t_bank(n)[:, c0:HALF], ACT.Copy).then_inc(S["t_hi"], 1)
                        if not fill and 0 <= n - WO_FROM < 2 * KB:
                            wo_hi(n - WO_FROM)
                    if kind == "O":
                        hh = UNITS[u][0]
                        act.wait_ge(S["pv_done"], p * N_T + LAST_T[u])
                        act.wait_ge(S["o_ready"], p * 4 + u)
                        A(oL[hh * HD:(hh + 1) * HD, :], pb[O_BANK][(1 - hh) * HD:(2 - hh) * HD, :], ACT.Copy).then_inc(S["ol_ready"], 1)
                    if exp_now:
                        exponent(p, *exp_now)

            def conv_back(b, c):
                for dst, src in ((ych, spill_h), (ycl, spill_l)):
                    nc.scalar.dma_start(dst[:, c].bitcast(F32), src.rearrange("(c p) s -> p c s", p=P)[:, c]).then_inc(conv_back_loaded[b], 16)

            def wo_hi(m):
                k, hf = divmod(m, 2)
                act.wait_ge(wo_loaded[m % WO_RAW], 16 * (m // WO_RAW + 1))
                A(WOh[:, k, hf * HALF:(hf + 1) * HALF], wo_raw[:, m % WO_RAW, :], ACT.Copy).then_inc(S["wo_hi"], 1)

            for t in range(TILES):
                copy_qkv(0, t)
                if t < NSEL:
                    sign_keys(t)
            act.wait_ge(S["counted"], 2 * BITS)
            act.wait_ge(S["cand_ready"], 2 * BITS + 2)
            act.wait_ge(S["bias_ready"], NSEL)
            act.wait_ge(S["y_lo"], 2 * CT)
            act.wait_ge(S["spilled"], 64 * (CT + 1))
            with act.Fori(0, PAIRS - 1) as p:
                pair_body(p, True)
            act.wait_ge(S["qkv_psum"], TILES * PAIRS)
            conv_back(0, slice(0, 3))
            pair_body(PAIRS - 1, False)

            act.wait_ge(S["o_ready"], 4 * PAIRS)
            act.wait_ge(S["pv_done"], PAIRS * N_T)
            for a in range(4):
                q = slice(2 * P * a, 2 * P * (a + 1))
                A(yah[:, :, q], yb[:, :, q], ACT.Copy).then_inc(S["ya_hi"], 1)

            for t in range(TILES):
                for n in range(2):
                    g_i = 2 * t + n
                    act.wait_ge(S["out_psum"], g_i + 1)
                    if t >= 2:
                        act.wait_ge(S["out_sq"], 2 * t - 1)
                    A(sqo[:, n, :], out_bank(g_i), ACT.Square, accum_out=ss[:, g_i:g_i + 1]).then_inc(S["out_sq"], 1)
                    if n == 0:
                        act.wait_ge(S["out_sq"], 2 * t + 1)
                        A(nmax[:, t:t + 1], ss[:, 2 * t:2 * t + 1], ACT.Identity, bias=epsT[:], scale=1.0 / DM).then_inc(S["out_std"], 1)
                act.wait_ge(S["out_sq"], 2 * t + 2)
                act.wait_ge(S["out_std"], 2 * t + 1)
                A(std[:, t:t + 1], ss[:, 2 * t + 1:2 * t + 2], ACT.Sqrt, bias=nmax[:, t:t + 1], scale=1.0 / DM).then_inc(S["out_std"], 1)

        @block.vector
        def _(dve):
            V = nc.vector

            V.memset(bias[:, 0:BIAS_OFF[FIRST_SEL]], 0.0)
            V.memset(thr[:, 0:len(DVE_SEL)], float(TOPK))
            for i in ACT_SEL:
                V.memset(thr[:, SEL_COL[i]:SEL_COL[i] + 1], float(2 * TOPK - P * (i + 1)))

            def scale_rows(t):
                dve.wait_ge(S["std_ready"], t + 1)
                V.reciprocal(rstd[:, t:t + 1], std[:, t:t + 1]).then_inc(S["rstd_ready"], 1)
                dve.wait_ge(S["rstd_ready"], t + 1)
                if t >= 2:
                    dve.wait_ge(S["xT_psum"], 2 * (t - 1))
                V.scalar_tensor_tensor(xs[:, t % 2, :], xin[:, t % 2, :], rstd[:, t:t + 1], gB[:], ALU.mult, ALU.mult).then_inc(S["xs_ready"], 1)

            dve.wait_ge(S["gains_loaded"], 16)
            scale_rows(0)
            for t in range(TILES):
                if t < 2:
                    dve.wait_ge(S["idx_w_hi"], t + 1)
                    h = slice(4 * t, 4 * t + 4)
                    V.tensor_tensor(WiL[:, h, :], WiR[:, h, :], WiH[:, h, :].bitcast(F32), ALU.subtract).then_inc(S["idx_w_lo"], 1)
                if t + 1 < TILES:
                    scale_rows(t + 1)
                for b in range(2):
                    n = 2 * t + b
                    dve.wait_ge(S["xT_hi"], n + 1)
                    d = (slice(None), slice(4 * b, 4 * b + 4), slice(t * P, (t + 1) * P))
                    V.tensor_tensor(xTl[d], pb[n % 4][:].rearrange("p (k s) -> p k s", k=4), xTh[d].bitcast(F32), ALU.subtract).then_inc(S["xT_lo"], 1)

            def rotate(src, rtmp, a, segs, at0):
                tt = slice(4 * a, 4 * a + 4)
                c = cosT[:, tt, :].unsqueeze(2).to_broadcast((P, 4, segs, RH))
                s = sinT[:, tt, :].unsqueeze(2).to_broadcast((P, 4, segs, RH))
                v = src[:, tt, 0:segs * HD].rearrange("p t (s d) -> p t s d", d=HD)
                x1, x2 = v[:, :, :, 0:RH], v[:, :, :, RH:ROT]
                r1, r2 = (rtmp[:, b, 0:4 * segs * RH].rearrange("p (t s d) -> p t s d", t=4, s=segs) for b in range(2))
                st = S["rope_step"]
                dve.wait_ge(st, at0)
                V.tensor_tensor(r1, x2, s, ALU.mult).then_inc(st, 1)
                V.tensor_tensor(r2, x1, s, ALU.mult).then_inc(st, 1)
                dve.wait_ge(st, at0 + 2)
                V.tensor_tensor(x1, x1, c, ALU.mult).then_inc(st, 1)
                V.tensor_tensor(x2, x2, c, ALU.mult).then_inc(st, 1)
                dve.wait_ge(st, at0 + 4)
                V.tensor_tensor(x1, x1, r1, ALU.subtract).then_inc(st, 1)
                V.tensor_tensor(x2, x2, r2, ALU.add).then_inc(st, 1)

            dve.wait_ge(S["consts_loaded"], 16 * (2 + CT))
            for a in range(2):
                dve.wait_ge(S["iq_ready"], 4 * a + 4)
                rotate(iq, rtI, a, IH + 1, 6 * a)
            V.tensor_copy(wI[:], iq[:, :, IDXC - IH:IDXC]).then_inc(S["wI_ready"], 1)

            def lo_part(dst, bank, hi):
                return V.tensor_tensor(dst, bank, hi.bitcast(F32), ALU.subtract)

            for n, (a, h) in enumerate(IDUP):
                cols = slice(a * HALF, (a + 1) * HALF)
                dve.wait_ge(S["idup_hi"], n + 1)
                if h == IH:
                    lo_part(KLI[:, cols], pb[6 + n % 2][:], KHI[:, cols]).then_inc(S["idup_lo"], 1)
                else:
                    lo_part(QSI[HD:P, h, cols], pb[6 + n % 2][HD:P, :], QSI[HD:P, h, cols]).then_inc(S["idup_lo"], 1)
            dve.wait_ge(S["wI_ready"], 1)
            kn = 0
            for n, (i, h, c) in enumerate(LOGITS):
                c0, c1 = chunk(i, c)
                dst = key[:, KEY_OFF[i] + c0:KEY_OFF[i] + c1]
                src = rl[:, n % RELU, 0:c1 - c0]
                if h > 0:
                    dve.wait_ge(S["relu_ready"], n + 1)
                    if h == 1:
                        dve.wait_ge(S["first_score"], sum(1 for ii, hh, cc in LOGITS if hh == 0 and (ii, cc) <= (i, c)))
                    else:
                        dve.wait_ge(S["score_step"], steps_until(n, False))
                    V.scalar_tensor_tensor(dst, src, wI[:, i, h:h + 1], dst, ALU.mult, ALU.add).then_inc(S["score_step"], 1)
                L = P * (i + 1)
                if h == IH - 1 and c1 == L:
                    kk = key[:, KEY_OFF[i]:KEY_OFF[i] + L]
                    dve.wait_ge(S["score_step"], steps_until(n + 1, False))
                    V.memset(kk[0:CHUNK, L - CHUNK:L], -3.4028235e38).then_inc(S["key_step"], 1)
                    dve.wait_ge(S["key_step"], kn + 1)
                    V.tensor_scalar(kt[:, 0:L], kk.bitcast(I32), 31, 0x7fffffff, ALU.arith_shift_right, ALU.bitwise_and).then_inc(S["key_step"], 1)
                    dve.wait_ge(S["key_step"], kn + 2)
                    V.tensor_tensor(kk.bitcast(I32), kk.bitcast(I32), kt[:, 0:L], ALU.bitwise_xor).then_inc(S["key_step"], 1)
                    kn += 3

            SM = S["small_step"]

            def start_search(c0, at):
                V.memset(cand[:], c0).then_inc(SM, 1)
                V.memset(step[:], 2.0 ** (BITS - 1)).then_inc(SM, 1)
                dve.wait_ge(SM, at + 2)
                V.tensor_scalar(nb[:], cand[:], -1.0, 0.5, ALU.mult, ALU.add).then_inc(S["cand_ready"], 1)

            def count(step_no, low):
                at = 2 + 5 * step_no + (3 if low else 0)
                dve.wait_ge(SM, at)
                V.scalar_tensor_tensor(cm[:], step[:], -0.5, cand[:], ALU.mult, ALU.add).then_inc(SM, 1)
                for i in DVE_SEL:
                    L, k0, c, jo = P * (i + 1), KEY_OFF[i], SEL_COL[i], JUNK_OFF[i]
                    src = key[:, k0:k0 + L] if low else key[:, k0:k0 + L].bitcast(I16)[:, 1::2]
                    last = V.tensor_scalar(jd[:, jo:jo + L], src, cand[:, c:c + 1], None, ALU.is_ge, ALU.add, accum_out=cnt[:, c:c + 1])
                last.then_inc(SM, 1)

            def decide(step_no, low):
                at = 2 + 5 * step_no + (3 if low else 0)
                dve.wait_ge(S["counted"], step_no + 1)
                dve.wait_ge(SM, at + 2)
                V.tensor_tensor(ge[:], cnt[:], thr[:], ALU.is_ge).then_inc(SM, 1)
                dve.wait_ge(SM, at + 3)
                V.scalar_tensor_tensor(cand[:], ge[:], step[:, 0:1], cm[:], ALU.mult, ALU.add).then_inc(SM, 1)
                dve.wait_ge(SM, at + 4)
                V.tensor_scalar(nb[:], cand[:], -1.0, 0.5, ALU.mult, ALU.add).then_inc(S["cand_ready"], 1)
                V.tensor_scalar(step[:], step[:], 0.5, None, ALU.mult).then_inc(SM, 1)

            def conv_body(it, low):
                dve.wait_ge(SM, 2 + 5 * GRP * it + (3 if low else 0))
                V.tensor_copy(cwb[:].unsqueeze(1), cw[:, bass.ds(it, 1), :]).then_inc(S["taps_ready"], 1)
                CS, BR = S["conv_step"], S["bank_read"]
                for gi in range(GRP):
                    j, n = divmod(gi, 2)
                    o = n * HALF
                    count(it * GRP + gi, low)
                    if j == 1:
                        dve.wait_ge(S["h_ready"], it * 2 + n + 1)
                        dve.wait_ge(S["grp_psum"], it * GRP + gi + 1)
                        V.tensor_tensor(uS[:, 2 + o:2 + o + HALF], conv_bank(gi), hS[:, n, :], ALU.mult).then_inc(BR, 1)
                        dve.wait_ge(BR, it * 6 + n + 1)
                        if n == 0:
                            dve.wait_ge(S["taps_ready"], it + 1)
                        V.tensor_scalar(yS[:, n, :], uS[:, 2 + o:2 + o + HALF], cwb[:, 2:3], None, ALU.mult).then_inc(CS, 1)
                    if j == 3:
                        dve.wait_ge(S["grp_psum"], it * GRP + gi + 1)
                        dve.wait_ge(CS, it * 6 + 3 * n + 3)
                        V.tensor_tensor(yo[:, n, :], conv_bank(gi), yS[:, n, :], ALU.mult).then_inc(BR, 1)
                        dve.wait_ge(BR, it * 6 + 5 + n)
                        V.scalar_tensor_tensor(yo[:, n, :], yo[:, n, :], 0.5, gz[:, n, :], ALU.mult, ALU.mult).then_inc(S["y_ready"], 1)
                    decide(it * GRP + gi, low)
                    if j == 1:
                        dve.wait_ge(CS, it * 6 + 3 * n + 1)
                        V.scalar_tensor_tensor(yS[:, n, :], uS[:, 1 + o:1 + o + HALF], cwb[:, 1:2], yS[:, n, :], ALU.mult, ALU.add).then_inc(CS, 1)
                        dve.wait_ge(CS, it * 6 + 3 * n + 2)
                        V.scalar_tensor_tensor(yS[:, n, :], uS[:, o:o + HALF], cwb[:, 0:1], yS[:, n, :], ALU.mult, ALU.add).then_inc(CS, 1)
                    if j == 2:
                        dve.wait_ge(S["tanh_ready"], it * 2 + n + 1)
                        V.scalar_tensor_tensor(gz[:, n, :], tz[:, n, :], 1.0, conv_bank(gi), ALU.add, ALU.mult).then_inc(BR, 1)
                    if j == 3:
                        dve.wait_ge(S["y_hi"], it * 2 + n + 1)
                        dve.wait_ge(S["spilled"], (it + 1) * 64)
                        V.tensor_tensor(yl[:, n, :], yo[:, n, :], yh[:, n, :].bitcast(F32), ALU.subtract).then_inc(S["y_lo"], 1)

            dve.wait_ge(S["key_step"], kn)
            V.memset(uS[:, 0:2], 0.0)
            start_search(0.0, 0)
            with dve.Fori(0, CT // 2) as it:
                conv_body(it, False)
            at = 2 + 5 * BITS
            dve.wait_ge(SM, at)
            V.tensor_scalar(need[:], cand[:], -65536.0, 32768.0, ALU.mult, ALU.add).then_inc(SM, 1)
            for n, i in enumerate(SEL_TILES):
                L, k0, c = P * (i + 1), KEY_OFF[i], SEL_COL[i]
                kk = key[:, k0:k0 + L]
                dve.wait_ge(S["kd_ready"], n + 1)
                V.tensor_tensor(kk, kd[:, n % 2, 0:L], kk.bitcast(U16)[:, 0::2], ALU.add).then_inc(S["key_step"], 1)
                kn += 1
            dve.wait_ge(S["key_step"], kn)
            start_search(2.0 ** (BITS - 1), at + 1)
            with dve.Fori(CT // 2, CT) as it:
                conv_body(it, True)

            def select(n):
                i = SEL_TILES[n]
                L, k0, c = P * (i + 1), KEY_OFF[i], SEL_COL[i]
                st, at = S["sel_step"], 5 * n + 1
                if n == 0:
                    dve.wait_ge(SM, 2 + 10 * BITS + 3)
                    V.tensor_scalar(cm[:], cand[:], -0.5, None, ALU.add).then_inc(st, 1)
                    dve.wait_ge(st, 1)
                if n >= 1:
                    dve.wait_ge(S["bias_ready"], n)
                E, C = mE[:, 0:L], mC[:, 0:L]
                V.tensor_scalar(E, key[:, k0:k0 + L], cm[:, c:c + 1], None, ALU.is_equal).then_inc(st, 1)
                dve.wait_ge(st, at + 1)
                V.tensor_tensor_scan(C, E, zero[:].to_broadcast((P, L)), 0.0, ALU.add, ALU.add).then_inc(st, 1)
                dve.wait_ge(S["sign_ready"], n + 1)
                V.tensor_scalar(need[:, c:c + 1], sgs[:, c:c + 1], -0.5, float(TOPK - L / 2), ALU.mult, ALU.add).then_inc(st, 1)
                dve.wait_ge(st, at + 3)
                V.scalar_tensor_tensor(need[:, c:c + 1], C[:, L - 1:L], 0.5, need[:, c:c + 1], ALU.mult, ALU.add).then_inc(st, 1)
                dve.wait_ge(st, at + 4)
                V.scalar_tensor_tensor(E, C, need[:, c:c + 1], mS[:, n % 2, 0:L], ALU.is_gt, ALU.subtract).then_inc(st, 1)
                dve.wait_ge(st, at + 5)
                V.tensor_scalar(bias[:, BIAS_OFF[i]:BIAS_OFF[i] + L], E, 0.5, -BIG, ALU.is_gt, ALU.mult).then_inc(S["bias_ready"], 1)

            def rotate_pair(p, a):
                dve.wait_ge(S["qkv_ready"], p * TILES + 4 * a + 4)
                rotate(qkv, rtP, a, 4, 12 + p * 12 + 6 * a)

            def invert(p, n, i):
                dve.wait_ge(S["p_ready"], p * N_S + n + 1)
                V.reciprocal(rinv[:, i:i + 1], rsum[:, i:i + 1]).then_inc(S["p_sum_inv"], 1)

            def pair_body(p, fill):
                pend = []
                for kind, u, j in PLAN if fill else LAST_PLAN:
                    if kind in "ZFV" or (kind in "CR" and not fill):
                        continue
                    if kind == "T" and j == 0:
                        for _, n, i in pend:
                            invert(p, n, i)
                        pend = []
                    due, pend = [x for x in pend if x[0] == 0], [(x[0] - 1,) + x[1:] for x in pend if x[0] > 0]
                    if kind == "R":
                        rotate_pair(p + 1, u)
                    if kind == "W":
                        dve.wait_ge(S["v_hi"], p + 1)
                        lo_part(VS[:, :, 1:3, :], qkv[:, :, 2 * P:3 * P].rearrange("p t (h d) -> p t h d", h=2), VS[:, :, 0::3, :]).then_inc(S["v_lo"], 1)
                    if kind == "G":
                        dve.wait_ge(S["tanh_ready"], 2 * CT + 2 * p + u + 1)
                        V.scalar_tensor_tensor(gate[:, u, :], gate[:, u, :], 1.0, pb[u][:], ALU.add, ALU.mult).then_inc(S["gate_ready"], 1)
                    if kind == "D":
                        a, w, hh = DUP[u]
                        cols = slice(a * HALF, (a + 1) * HALF)
                        dve.wait_ge(S["dup_hi"], p * len(DUP) + u + 1)
                        if w:
                            lo_part(KL[:, hh, cols], t_bank(u)[:], KH[:, hh, cols]).then_inc(S["dup_lo"], 1)
                        else:
                            lo_part(QS[HD:P, hh, cols], t_bank(u)[HD:P, :], QS[HD:P, hh, cols]).then_inc(S["dup_lo"], 1)
                    if kind == "S":
                        gg = UNITS[u][1]
                        n = S_OF[(u, j)]
                        at, L = BIAS_OFF[j] - BIAS_OFF[4 * gg], P * (j + 1)
                        b0 = s_bank(j)
                        dve.wait_ge(S["s_psum"], p * N_S + n + 1)
                        if u >= 2:
                            dve.wait_ge(S["t_psum"], p * N_T + LAST_T[u - 2])
                        dve.sem_inc(S["waited_dve"], 1)
                        V.tensor_tensor_reduce(PPG[gg][:, at:at + L], banks[:, b0:b0 + 1 + gg, :].rearrange("p b s -> p (b s)")[:, 0:L],
                                               bias[:, BIAS_OFF[j]:BIAS_OFF[j] + L], -SCALE, BIG, ALU.add, ALU.min,
                                               nmax[:, j:j + 1]).then_inc(S["s_masked"], 1)
                        pend.append((INV_LAG, n, j))
                    if kind == "T":
                        gg = UNITS[u][1]
                        n = T_OF[(u, j)]
                        c0 = max(j - 4 * gg, 0) * P
                        dve.wait_ge(S["t_hi"], p * N_T + n + 1)
                        lo_part(PTl[:, n % T_RING, c0:HALF], t_bank(n)[:, c0:HALF], PTh[:, n % T_RING, c0:HALF]).then_inc(S["t_lo"], 1)
                    if kind == "O":
                        hh, gg = UNITS[u]
                        rows = slice(hh * HD, (hh + 1) * HD)
                        if u == 0:
                            dve.wait_ge(S["gate_ready"], 2 * p + 2)
                        dve.wait_ge(S["ol_ready"], p * 4 + u + 1)
                        V.scalar_tensor_tensor(oL[rows, :], pb[O_BANK][rows, :], 1.0, oL[rows, :], ALU.mult, ALU.add).then_inc(S["o_summed"], 1)
                        dve.wait_ge(S["o_summed"], p * 4 + u + 1)
                        V.scalar_tensor_tensor(yb[rows, bass.ds(p, 1), gg * HALF:(gg + 1) * HALF].rearrange("p a b -> p (a b)"),
                                               oL[rows, :], 0.5, gate[rows, gg, :], ALU.mult, ALU.mult).then_inc(S["o_ready"], 1)
                    for _, n, i in due:
                        invert(p, n, i)

            for t in range(TILES):
                if t % 4 == 3:
                    rotate_pair(0, t // 4)
                if t < NSEL:
                    select(t)
            dve.wait_ge(S["bias_ready"], NSEL)
            for i in range(TILES):
                e = BIAS_OFF[i] + P * (i + 1)
                last = V.memset(bias[0:CHUNK, e - CHUNK:e], -BIG)
            last.then_inc(S["diag_ready"], 1)
            dve.wait_ge(S["diag_ready"], 1)
            with dve.Fori(0, PAIRS - 1) as p:
                pair_body(p, True)
            pair_body(PAIRS - 1, False)

            dve.wait_ge(S["o_ready"], 4 * PAIRS)
            for a in range(4):
                q = slice(2 * P * a, 2 * P * (a + 1))
                dve.wait_ge(S["ya_hi"], a + 1)
                lo_part(yal[:, :, q], yb[:, :, q], yah[:, :, q]).then_inc(S["ya_lo"], 1)

            dve.wait_ge(S["gains_loaded"], 32)
            for t in range(TILES):
                dve.wait_ge(S["out_std"], 2 * t + 2)
                V.reciprocal(rstd[:, t:t + 1], std[:, t:t + 1]).then_inc(S["out_rstd"], 1)
                dve.wait_ge(S["out_rstd"], t + 1)
                if t >= 2:
                    dve.wait_ge(stored[t % 2], 32 * (t // 2))
                for n in range(2):
                    cols = slice(n * HALF, (n + 1) * HALF)
                    V.scalar_tensor_tensor(oS[:, t % 2, cols], out_bank(2 * t + n), rstd[:, t:t + 1], gP[:, cols], ALU.mult, ALU.mult).then_inc(S["out_scaled"], 1)
                    if n == 0:
                        dve.wait_ge(xr_loaded[t % 2], 16 * (t // 2 + 1))
                    dve.wait_ge(S["out_scaled"], 2 * t + n + 1)
                    V.tensor_tensor(oS[:, t % 2, cols], oS[:, t % 2, cols], xr[:, t % 2, cols], ALU.add).then_inc(S["out_ready"], 1)


def kernel(x, norm_pre_g, w_in, conv_w, w_out, norm_post_g):
    import concourse.bacc as bacc
    from concourse.bass_utils import run_bass_kernel_spmd

    inv = np.power(np.float32(500000.0), -np.arange(RH, dtype=np.float32) / np.float32(RH)).astype(np.float32)
    ang = np.arange(SEQ, dtype=np.float32)[:, None] * inv[None, :]
    rope = np.stack([np.cos(ang), np.sin(ang)]).astype(np.float32)
    arrays = {
        "x": np.ascontiguousarray(x[0]), "w_in": np.ascontiguousarray(w_in[0]), "w_out": np.ascontiguousarray(w_out[0]),
        "conv_w": np.ascontiguousarray(conv_w[0]), "g_pre": np.ascontiguousarray(norm_pre_g),
        "g_post": np.ascontiguousarray(norm_post_g), "rope": rope,
    }
    nc = bacc.Bacc("TRN2", target_bir_lowering=False, num_devices=1)
    aps = {n: nc.dram_tensor(n, a.shape, mybir.dt.from_np(a.dtype), kind="ExternalInput").ap() for n, a in arrays.items()}
    out = nc.dram_tensor("out", (SEQ, DM), F32, kind="ExternalOutput").ap()
    build(nc, aps["x"], aps["w_in"], aps["w_out"], aps["conv_w"], aps["g_pre"], aps["g_post"], aps["rope"], out)
    result = run_bass_kernel_spmd(nc, [arrays], core_ids=[0])
    return np.asarray(result.results[0]["out"]).reshape(1, SEQ, DM)
```
